# Optimizing a Trainium2 kernel written in Bass

```python
import math
import jax, jax.numpy as jnp
from jax import lax
import numpy as np

D_MODEL = 2048
BATCH = 1
SEQ = 256
DEPTH = 1

CHUNK = 64
N_MIXERS = 2
EPS = 1e-6

GLA_HEADS = 4
GLA_KEY_WIDTH = D_MODEL // 2
GLA_VAL_WIDTH = D_MODEL
GLA_DK = GLA_KEY_WIDTH // GLA_HEADS
GLA_DV = GLA_VAL_WIDTH // GLA_HEADS
GLA_GATE_RANK = 16
GLA_GATE_TEMP = 16.0
GLA_IN_WIDTH = 2 * GLA_KEY_WIDTH + 2 * GLA_VAL_WIDTH + GLA_GATE_RANK

S5_WIDTH = D_MODEL // 2
S5_GROUP = 16
S5_GROUPS = S5_WIDTH // S5_GROUP
S5_STATE = 64
S5_DT_MIN = 1e-3
S5_DT_MAX = 1e-1
S5_EIG_CLIP = -1e-4

MLP_HIDDEN = 4 * D_MODEL


def _rmsnorm(x, g):
    xf = x.astype(jnp.float32)
    y = xf * lax.rsqrt(jnp.mean(xf * xf, axis=-1, keepdims=True) + EPS)
    return (y * g.astype(jnp.float32)).astype(x.dtype)

def _gla_mixer(h, w_in, w_gate_up, b_gate, o_norm, w_out):
    bsz, seq, _ = h.shape
    nc = seq // CHUNK
    proj = h @ w_in
    q, k, v, r, g_low = jnp.split(
        proj,
        [GLA_KEY_WIDTH, 2 * GLA_KEY_WIDTH, 2 * GLA_KEY_WIDTH + GLA_VAL_WIDTH,
         2 * GLA_KEY_WIDTH + 2 * GLA_VAL_WIDTH], axis=-1)
    log_a = jax.nn.log_sigmoid((g_low @ w_gate_up + b_gate).astype(jnp.float32)) / GLA_GATE_TEMP

    def to_chunks(t, dh):
        return t.reshape(bsz, nc, CHUNK, GLA_HEADS, dh).transpose(1, 0, 3, 2, 4).astype(jnp.float32)

    qc = to_chunks(q, GLA_DK) * (GLA_DK ** -0.5)
    kc = to_chunks(k, GLA_DK)
    vc = to_chunks(v, GLA_DV)
    ac = to_chunks(log_a, GLA_DK)
    cum = jnp.cumsum(ac, axis=3)
    total = cum[:, :, :, -1:, :]
    k_dec = kc * jnp.exp(total - cum)
    chunk_decay = jnp.exp(total[:, :, :, 0, :])

    def step(state, xs):
        q_c, k_c, v_c, d_c = xs
        state = d_c[..., None] * state + jnp.einsum('bhck,bhcv->bhkv', k_c, v_c)
        return state, jnp.einsum('bhck,bhkv->bhcv', q_c, state)

    s0 = jnp.zeros((bsz, GLA_HEADS, GLA_DK, GLA_DV), jnp.float32)
    _, o = lax.scan(step, s0, (qc, k_dec, vc, chunk_decay))
    o = o * lax.rsqrt(jnp.mean(o * o, axis=-1, keepdims=True) + EPS) * o_norm.astype(jnp.float32)
    o = o.transpose(1, 0, 3, 2, 4).reshape(bsz, seq, GLA_VAL_WIDTH).astype(h.dtype)
    return (o * jax.nn.silu(r)) @ w_out

def _s5_mixer(h, w_in, lam_re, lam_im, log_dt, b_re, b_im, c_re, c_im, d_skip, w_out):
    bsz, seq, _ = h.shape
    u = (h @ w_in).astype(jnp.float32)
    ug = u.reshape(bsz, seq, S5_GROUPS, S5_GROUP)
    lr = jnp.minimum(lam_re.astype(jnp.float32), S5_EIG_CLIP)
    li = lam_im.astype(jnp.float32)
    dt = jnp.exp(log_dt.astype(jnp.float32))[:, None]
    mag = jnp.exp(lr * dt)
    ang = li * dt
    ab_re = mag * jnp.cos(ang)
    ab_im = mag * jnp.sin(ang)
    den = lr * lr + li * li
    nr = ab_re - 1.0
    f_re = (nr * lr + ab_im * li) / den
    f_im = (ab_im * lr - nr * li) / den
    br = b_re.astype(jnp.float32)
    bi = b_im.astype(jnp.float32)
    bb_re = f_re[..., None] * br - f_im[..., None] * bi
    bb_im = f_re[..., None] * bi + f_im[..., None] * br
    bu_re = jnp.einsum('gnc,blgc->blgn', bb_re, ug)
    bu_im = jnp.einsum('gnc,blgc->blgn', bb_im, ug)
    a_re = jnp.broadcast_to(ab_re, bu_re.shape)
    a_im = jnp.broadcast_to(ab_im, bu_im.shape)

    def combine(e1, e2):
        a1r, a1i, b1r, b1i = e1
        a2r, a2i, b2r, b2i = e2
        return (a2r * a1r - a2i * a1i,
                a2r * a1i + a2i * a1r,
                a2r * b1r - a2i * b1i + b2r,
                a2r * b1i + a2i * b1r + b2i)

    _, _, x_re, x_im = lax.associative_scan(combine, (a_re, a_im, bu_re, bu_im), axis=1)
    y = (jnp.einsum('gcn,blgn->blgc', c_re.astype(jnp.float32), x_re)
         - jnp.einsum('gcn,blgn->blgc', c_im.astype(jnp.float32), x_im))
    y = y.reshape(bsz, seq, S5_WIDTH) + d_skip.astype(jnp.float32) * u
    y = jax.nn.gelu(y).astype(h.dtype)
    val, gate = jnp.split(y @ w_out, 2, axis=-1)
    return val * jax.nn.sigmoid(gate)

def _sq_relu_mlp(h, w_up, w_down):
    a = jax.nn.relu(h @ w_up)
    return (a * a) @ w_down

def first_inputs(seed: int = 0) -> dict:
    key = jax.random.key(seed)
    ks = jax.random.split(key, 24)
    n_gla = len(range(0, DEPTH, N_MIXERS))
    n_s5 = len(range(1, DEPTH, N_MIXERS))
    res_scale = (2 * DEPTH) ** -0.5

    def nrm(k, shape, scale):
        return jax.random.normal(k, shape, jnp.float32) * scale

    def gain(k, shape):
        return 1.0 + 0.02 * jax.random.normal(k, shape, jnp.float32)

    lam_im0 = math.pi * jnp.arange(S5_STATE, dtype=jnp.float32)
    return {
        'x': jax.random.normal(ks[0], (BATCH, SEQ, D_MODEL), jnp.float32),
        'gla_norm': gain(ks[1], (n_gla, D_MODEL)),
        'gla_w_in': nrm(ks[2], (n_gla, D_MODEL, GLA_IN_WIDTH), D_MODEL ** -0.5),
        'gla_w_gate_up': nrm(ks[3], (n_gla, GLA_GATE_RANK, GLA_KEY_WIDTH), GLA_GATE_RANK ** -0.5),
        'gla_b_gate': 1.0 + 0.1 * jax.random.normal(ks[4], (n_gla, GLA_KEY_WIDTH), jnp.float32),
        'gla_o_norm': gain(ks[5], (n_gla, GLA_DV)),
        'gla_w_out': nrm(ks[6], (n_gla, GLA_VAL_WIDTH, D_MODEL), GLA_VAL_WIDTH ** -0.5 * res_scale),
        's5_norm': gain(ks[7], (n_s5, D_MODEL)),
        's5_w_in': nrm(ks[8], (n_s5, D_MODEL, S5_WIDTH), D_MODEL ** -0.5),
        's5_lam_re': -0.5 + 0.01 * jax.random.normal(ks[9], (n_s5, S5_GROUPS, S5_STATE), jnp.float32),
        's5_lam_im': lam_im0 + 0.01 * jax.random.normal(ks[10], (n_s5, S5_GROUPS, S5_STATE), jnp.float32),
        's5_log_dt': jax.random.uniform(ks[11], (n_s5, S5_GROUPS), jnp.float32,
                                        minval=math.log(S5_DT_MIN), maxval=math.log(S5_DT_MAX)),
        's5_b_re': nrm(ks[12], (n_s5, S5_GROUPS, S5_STATE, S5_GROUP), (2 * S5_GROUP) ** -0.5),
        's5_b_im': nrm(ks[13], (n_s5, S5_GROUPS, S5_STATE, S5_GROUP), (2 * S5_GROUP) ** -0.5),
        's5_c_re': nrm(ks[14], (n_s5, S5_GROUPS, S5_GROUP, S5_STATE), (2 * S5_STATE) ** -0.5),
        's5_c_im': nrm(ks[15], (n_s5, S5_GROUPS, S5_GROUP, S5_STATE), (2 * S5_STATE) ** -0.5),
        's5_d': jax.random.normal(ks[16], (n_s5, S5_WIDTH), jnp.float32),
        's5_w_out': nrm(ks[17], (n_s5, S5_WIDTH, 2 * D_MODEL), S5_WIDTH ** -0.5 * res_scale),
        'mlp_norm': gain(ks[18], (DEPTH, D_MODEL)),
        'mlp_w_up': nrm(ks[19], (DEPTH, D_MODEL, MLP_HIDDEN), D_MODEL ** -0.5),
        'mlp_w_down': nrm(ks[20], (DEPTH, MLP_HIDDEN, D_MODEL), MLP_HIDDEN ** -0.5 * res_scale),
        'final_norm': gain(ks[21], (D_MODEL,)),
    }

def first_block(x, gla_norm, gla_w_in, gla_w_gate_up, gla_b_gate, gla_o_norm, gla_w_out,
              s5_norm, s5_w_in, s5_lam_re, s5_lam_im, s5_log_dt, s5_b_re, s5_b_im,
              s5_c_re, s5_c_im, s5_d, s5_w_out, mlp_norm, mlp_w_up, mlp_w_down, final_norm):
    h = x
    for i in range(DEPTH):
        j = i // N_MIXERS
        if i % N_MIXERS == 0:
            h = h + _gla_mixer(_rmsnorm(h, gla_norm[j]), gla_w_in[j], gla_w_gate_up[j],
                               gla_b_gate[j], gla_o_norm[j], gla_w_out[j])
        else:
            h = h + _s5_mixer(_rmsnorm(h, s5_norm[j]), s5_w_in[j], s5_lam_re[j], s5_lam_im[j],
                              s5_log_dt[j], s5_b_re[j], s5_b_im[j], s5_c_re[j], s5_c_im[j],
                              s5_d[j], s5_w_out[j])
        h = h + _sq_relu_mlp(_rmsnorm(h, mlp_norm[i]), mlp_w_up[i], mlp_w_down[i])
    return _rmsnorm(h, final_norm)


N_HEADS = 8
HEAD_DIM = 128
ATTN_W = N_HEADS * HEAD_DIM
MOBA_BLOCK = 256
MOBA_TOPK = 3
MOBA_QCHUNK = 64
N_BUCKETS = 32
MAX_DISTANCE = 128
LRU_W = D_MODEL // 2
LRU_BLOCKS = 8
LRU_BW = LRU_W // LRU_BLOCKS
LRU_CONV = 4
LRU_C = 8.0
SC_W = D_MODEL // 2
SC_CONV = 3
D_FF = 4 * D_MODEL
N_BRANCH = 3
IN_SPLITS = (ATTN_W, ATTN_W, ATTN_W, LRU_W, LRU_W, SC_W, SC_W, SC_W, N_BRANCH * D_MODEL)
N_IN = sum(IN_SPLITS)


def rms_norm(x, g):
    xf = x.astype(jnp.float32)
    y = xf * lax.rsqrt(jnp.mean(xf * xf, axis=-1, keepdims=True) + EPS)
    return (y * g.astype(jnp.float32)).astype(x.dtype)

def causal_depthwise_conv(x, w):
    k = w.shape[0]
    return lax.conv_general_dilated(
        x, w[:, None, :].astype(x.dtype), window_strides=(1,), padding=[(k - 1, 0)],
        dimension_numbers=('NWC', 'WIO', 'NWC'), feature_group_count=x.shape[-1])

def t5_bucket(dist):
    n = jnp.maximum(dist, 0)
    max_exact = N_BUCKETS // 2
    nf = jnp.maximum(n, 1).astype(jnp.float32)
    large = max_exact + (jnp.log(nf / max_exact) / math.log(MAX_DISTANCE / max_exact)
                         * (N_BUCKETS - max_exact)).astype(jnp.int32)
    large = jnp.minimum(large, N_BUCKETS - 1)
    return jnp.where(n < max_exact, n, large)

def moba_attention(q, k, v, rel_table):
    bsz, seq, n_heads, d_head = q.shape
    n_blk = -(-seq // MOBA_BLOCK)
    s_pad = n_blk * MOBA_BLOCK
    topk = min(MOBA_TOPK, n_blk)
    pad = ((0, 0), (0, s_pad - seq), (0, 0), (0, 0))
    qh = jnp.pad(q * (d_head ** -0.5), pad).transpose(0, 2, 1, 3)
    kh = jnp.pad(k, pad).transpose(0, 2, 1, 3)
    vh = jnp.pad(v, pad).transpose(0, 2, 1, 3)
    kb = kh.reshape(bsz, n_heads, n_blk, MOBA_BLOCK, d_head)
    vb = vh.reshape(bsz, n_heads, n_blk, MOBA_BLOCK, d_head)
    k_mean = jnp.mean(kb.astype(jnp.float32), axis=3)
    gate = jnp.einsum('bhsd,bhnd->bhsn', qh.astype(jnp.float32), k_mean)
    q_blk = jnp.arange(s_pad) // MOBA_BLOCK
    past = jnp.arange(n_blk)[None, :] < q_blk[:, None]
    gate = jnp.where(past, gate, -jnp.inf)
    _, sel = lax.top_k(gate, topk)
    slot_ok = jnp.arange(topk)[None, :] < q_blk[:, None]
    b_idx = jnp.arange(bsz)[:, None, None, None]
    h_idx = jnp.arange(n_heads)[None, :, None, None]
    tbl_hb = rel_table.T
    blk_pos = jnp.arange(MOBA_BLOCK)

    def chunk(c):
        start = c * MOBA_QCHUNK
        qc = lax.dynamic_slice_in_dim(qh, start, MOBA_QCHUNK, axis=2)
        sel_c = lax.dynamic_slice_in_dim(sel, start, MOBA_QCHUNK, axis=2)
        ok_c = lax.dynamic_slice_in_dim(slot_ok, start, MOBA_QCHUNK, axis=0)
        q_pos = start + jnp.arange(MOBA_QCHUNK)
        kg = kb[b_idx, h_idx, sel_c]
        vg = vb[b_idx, h_idx, sel_c]
        s_past = jnp.einsum('bhqd,bhqnkd->bhqnk', qc, kg, preferred_element_type=jnp.float32)
        k_pos = sel_c[..., None] * MOBA_BLOCK + blk_pos
        bkt = t5_bucket(q_pos[:, None, None] - k_pos)
        s_past = s_past + tbl_hb[h_idx[..., None], bkt]
        s_past = jnp.where(ok_c[:, :, None], s_past, -jnp.inf)
        own = start // MOBA_BLOCK
        k_own = lax.dynamic_index_in_dim(kb, own, axis=2, keepdims=False)
        v_own = lax.dynamic_index_in_dim(vb, own, axis=2, keepdims=False)
        s_own = jnp.einsum('bhqd,bhkd->bhqk', qc, k_own, preferred_element_type=jnp.float32)
        dist = q_pos[:, None] - (own * MOBA_BLOCK + blk_pos)[None, :]
        s_own = s_own + rel_table[t5_bucket(dist)].transpose(2, 0, 1)
        s_own = jnp.where(dist >= 0, s_own, -jnp.inf)
        logits = jnp.concatenate(
            [s_past.reshape(bsz, n_heads, MOBA_QCHUNK, topk * MOBA_BLOCK), s_own], axis=-1)
        p = jax.nn.softmax(logits, axis=-1)
        p_past = p[..., :topk * MOBA_BLOCK].reshape(bsz, n_heads, MOBA_QCHUNK, topk, MOBA_BLOCK)
        p_own = p[..., topk * MOBA_BLOCK:]
        o = (jnp.einsum('bhqnk,bhqnkd->bhqd', p_past.astype(vg.dtype), vg,
                        preferred_element_type=jnp.float32)
             + jnp.einsum('bhqk,bhkd->bhqd', p_own.astype(v_own.dtype), v_own,
                          preferred_element_type=jnp.float32))
        return o.astype(q.dtype)

    out = lax.map(chunk, jnp.arange(s_pad // MOBA_QCHUNK))
    out = out.transpose(1, 0, 3, 2, 4).reshape(bsz, s_pad, n_heads * d_head)
    return out[:, :seq]

def _lru_combine(c1, c2):
    a1, b1 = c1
    a2, b2 = c2
    return a1 * a2, a2 * b1 + b2

def rg_lru_branch(xr, gate_br, conv_w, conv_b, wa, ba, wx, bx, lam):
    xc = causal_depthwise_conv(xr, conv_w) + conv_b
    bsz, seq, width = xc.shape
    xg = xc.reshape(bsz, seq, LRU_BLOCKS, LRU_BW)
    r = jax.nn.sigmoid((jnp.einsum('bsgi,gij->bsgj', xg, wa).reshape(bsz, seq, width) + ba)
                       .astype(jnp.float32))
    i = jax.nn.sigmoid((jnp.einsum('bsgi,gij->bsgj', xg, wx).reshape(bsz, seq, width) + bx)
                       .astype(jnp.float32))
    log_a = -LRU_C * r * jax.nn.softplus(-lam.astype(jnp.float32))
    a = jnp.exp(log_a)
    mult = jnp.sqrt(-jnp.expm1(2.0 * log_a))
    u = mult * i * xc.astype(jnp.float32)
    _, h = lax.associative_scan(_lru_combine, (a, u), axis=1)
    return (h * jax.nn.gelu(gate_br.astype(jnp.float32))).astype(xr.dtype)

def short_conv_branch(b, c, xs, conv_w):
    return b * causal_depthwise_conv(c * xs, conv_w)

def second_inputs(seed: int = 0) -> dict:
    key = jax.random.key(seed)
    ks = jax.random.split(key, 24)
    f32 = jnp.float32
    nrm = lambda k, shape, fan_in: jax.random.normal(k, shape, f32) * (fan_in ** -0.5)
    u = jax.random.uniform(ks[12], (DEPTH, LRU_W), f32, minval=0.9, maxval=0.999)
    a_base = u ** (1.0 / LRU_C)
    lam = jnp.log(a_base) - jnp.log1p(-a_base)
    return {
        "x": jax.random.normal(ks[0], (BATCH, SEQ, D_MODEL), f32),
        "norm_mix_g": 1.0 + 0.02 * jax.random.normal(ks[1], (DEPTH, D_MODEL), f32),
        "w_in": nrm(ks[2], (DEPTH, D_MODEL, N_IN), D_MODEL),
        "gate_b": 0.02 * jax.random.normal(ks[3], (DEPTH, N_BRANCH * D_MODEL), f32),
        "rel_table": 0.1 * jax.random.normal(ks[4], (N_BUCKETS, N_HEADS), f32),
        "w_attn_o": nrm(ks[5], (DEPTH, ATTN_W, D_MODEL), ATTN_W),
        "lru_conv_w": nrm(ks[6], (DEPTH, LRU_CONV, LRU_W), LRU_CONV),
        "lru_conv_b": 0.02 * jax.random.normal(ks[7], (DEPTH, LRU_W), f32),
        "lru_wa": nrm(ks[8], (DEPTH, LRU_BLOCKS, LRU_BW, LRU_BW), LRU_BW),
        "lru_ba": 0.02 * jax.random.normal(ks[9], (DEPTH, LRU_W), f32),
        "lru_wx": nrm(ks[10], (DEPTH, LRU_BLOCKS, LRU_BW, LRU_BW), LRU_BW),
        "lru_bx": 0.02 * jax.random.normal(ks[11], (DEPTH, LRU_W), f32),
        "lru_lambda": lam,
        "w_lru_o": nrm(ks[13], (DEPTH, LRU_W, D_MODEL), LRU_W),
        "sc_conv_w": nrm(ks[14], (DEPTH, SC_CONV, SC_W), SC_CONV),
        "w_sc_o": nrm(ks[15], (DEPTH, SC_W, D_MODEL), SC_W),
        "w_out": nrm(ks[16], (DEPTH, D_MODEL, D_MODEL), D_MODEL),
        "norm_mlp_g": 1.0 + 0.02 * jax.random.normal(ks[17], (DEPTH, D_MODEL), f32),
        "w_mlp_up": nrm(ks[18], (DEPTH, D_MODEL, D_FF), D_MODEL),
        "w_mlp_down": nrm(ks[19], (DEPTH, D_FF, D_MODEL), D_FF),
        "final_g": 1.0 + 0.02 * jax.random.normal(ks[20], (D_MODEL,), f32),
    }

def second_block(x, norm_mix_g, w_in, gate_b, rel_table, w_attn_o, lru_conv_w, lru_conv_b,
              lru_wa, lru_ba, lru_wx, lru_bx, lru_lambda, w_lru_o, sc_conv_w, w_sc_o,
              w_out, norm_mlp_g, w_mlp_up, w_mlp_down, final_g):
    bsz, seq, _ = x.shape
    offs = np.cumsum(IN_SPLITS)[:-1].tolist()
    for l in range(DEPTH):
        h = rms_norm(x, norm_mix_g[l])
        proj = h @ w_in[l]
        q, k, v, xr, gr, sc_b, sc_c, sc_x, g_pre = jnp.split(proj, offs, axis=-1)
        heads = (bsz, seq, N_HEADS, HEAD_DIM)
        y_a = moba_attention(q.reshape(heads), k.reshape(heads), v.reshape(heads),
                             rel_table) @ w_attn_o[l]
        y_b = rg_lru_branch(xr, gr, lru_conv_w[l], lru_conv_b[l], lru_wa[l], lru_ba[l],
                            lru_wx[l], lru_bx[l], lru_lambda[l]) @ w_lru_o[l]
        y_c = short_conv_branch(sc_b, sc_c, sc_x, sc_conv_w[l]) @ w_sc_o[l]
        g_a, g_b, g_c = jnp.split(jax.nn.sigmoid(g_pre + gate_b[l]), N_BRANCH, axis=-1)
        x = x + (g_a * y_a + g_b * y_b + g_c * y_c) @ w_out[l]
        h = rms_norm(x, norm_mlp_g[l])
        x = x + jnp.square(jax.nn.relu(h @ w_mlp_up[l])) @ w_mlp_down[l]
    return rms_norm(x, final_g)


def setup_inputs(seed=0):
    out = dict(first_inputs(seed))
    for name, value in second_inputs(seed + 1).items():
        if name != "x":
            out[name + "_2"] = value
    return out


def reference(
    x, gla_norm, gla_w_in, gla_w_gate_up, gla_b_gate, gla_o_norm, gla_w_out, s5_norm, s5_w_in,
    s5_lam_re, s5_lam_im, s5_log_dt, s5_b_re, s5_b_im, s5_c_re, s5_c_im, s5_d, s5_w_out,
    mlp_norm, mlp_w_up, mlp_w_down, final_norm, norm_mix_g_2, w_in_2, gate_b_2, rel_table_2,
    w_attn_o_2, lru_conv_w_2, lru_conv_b_2, lru_wa_2, lru_ba_2, lru_wx_2, lru_bx_2,
    lru_lambda_2, w_lru_o_2, sc_conv_w_2, w_sc_o_2, w_out_2, norm_mlp_g_2, w_mlp_up_2,
    w_mlp_down_2, final_g_2,
):
    x = first_block(
        x, gla_norm, gla_w_in, gla_w_gate_up, gla_b_gate, gla_o_norm, gla_w_out, s5_norm,
        s5_w_in, s5_lam_re, s5_lam_im, s5_log_dt, s5_b_re, s5_b_im, s5_c_re, s5_c_im, s5_d,
        s5_w_out, mlp_norm, mlp_w_up, mlp_w_down, final_norm,
    )
    return second_block(
        x, norm_mix_g_2, w_in_2, gate_b_2, rel_table_2, w_attn_o_2, lru_conv_w_2, lru_conv_b_2,
        lru_wa_2, lru_ba_2, lru_wx_2, lru_bx_2, lru_lambda_2, w_lru_o_2, sc_conv_w_2, w_sc_o_2,
        w_out_2, norm_mlp_g_2, w_mlp_up_2, w_mlp_down_2, final_g_2,
    )


_drawn_inputs = setup_inputs


def setup_inputs(seed=0):
    import zlib

    import numpy as np

    out = dict(_drawn_inputs(seed))
    spreads = {}
    factors = {'gla_o_norm': 5.062,
     'mlp_norm': 2.989,
     'norm_mix_g_2': 2.793,
     'gate_b_2': 8.0,
     'rel_table_2': 6.578,
     'lru_ba_2': 64.0,
     'lru_bx_2': 28.693,
     'norm_mlp_g_2': 11.793,
     'final_g_2': 7.798,
     'lru_conv_b_2': 7.747}
    for name, (base, spread) in spreads.items():
        noise = np.random.default_rng([zlib.crc32(name.encode()), seed]).standard_normal(out[name].shape)
        drawn = base * np.exp(spread * noise) if base else spread * noise
        out[name] = __import__('jax').numpy.asarray(drawn.astype(out[name].dtype))
    for name, factor in factors.items():
        out[name] = (out[name] * factor).astype(out[name].dtype)
    return out
```

```python
from contextlib import ExitStack, contextmanager

import numpy as np

import concourse.bass as bass
from concourse import mybir

F32 = mybir.dt.float32
F32R = mybir.dt.float32r
ALU = mybir.AluOpType
ACT = mybir.ActivationFunctionType
AX_X = mybir.AxisListType.X

P = 128
T = 256
TT = T // P
D = 2048
KT = D // P
NB = 256
UK = 4
SLOTS = 4
PAIRS = KT // 2
EPS = 1e-6

HEADS, DK, DV, CHUNK = 4, 256, 512, 64
NCH = T // CHUNK
KEYW, VALW, RANK, TEMP = 1024, 2048, 16, 16.0
HID = 4 * D
NCK = HID // D
AH, AD = 8, 128
NBUCKET, MAXDIST = 32, 128
LW, CONV, SCONV = 1024, 4, 3
LKT = LW // P
NEG = -1e30
BW = 3 * P

STREAM = [("gk", 4, 4), ("gv", 8, 4), ("gq", 4, 4), ("gr", 8, 4), ("go", 8, 4), ("m1", 64, 4),
          ("q", 4, 4), ("k", 4, 4), ("v", 4, 4), ("xr", 4, 4), ("scc", 4, 4), ("scx", 4, 4),
          ("br", 4, 4), ("scb", 4, 4), ("mix", 48, 3), ("lo", 8, 4), ("m2", 64, 4)]
BLOCK0, ROUND0 = {}, {}
_b = _u = 0
for _n, _k, _c in STREAM:
    BLOCK0[_n], ROUND0[_n] = _b, _u // SLOTS
    assert _u % SLOTS == 0 and _b % 2 == 0
    _b, _u = _b + _k, _u + _k * _c
ROUNDS = _u // SLOTS
MIX_UNITS = (4, 2, 4, 2, 4, 2)
PAIR0 = {"x1": 0, "gr": 8, "xm1": 16, "h1": 24, "x2": 56, "ya": 64, "yb": 64, "yc": 68, "mix": 72,
         "xm2": 80, "h2": 88}
FINAL0 = PAIR0["h2"] + 32
FUN0 = {"gr": 0, "br": 8, "gate": 12}
ROWS = {}
_r = 0
for _n, _k in (("gla_norm", 16), ("mlp_norm", 16), ("final_norm", 16), ("norm_mix_g_2", 16),
               ("norm_mlp_g_2", 16), ("final_g_2", 16), ("gla_b_gate", 8), ("gla_o_norm", 4),
               ("lru_conv_b_2", 8), ("lru_ba_2", 8)):
    ROWS[_n] = (_r, _k)
    _r += _k
ROWS_A = _r
_r = P
for _n, _k in (("gate_b_2", 48), ("lru_conv_w_2", 32), ("lru_bx_2", 8), ("lru_lambda_2", 8),
               ("sc_conv_w_2", 24)):
    ROWS[_n] = (_r, _k)
    _r += _k
ROWS_B = _r - P
CHUNK_PAIRS = [(0, 1), (0, 2), (0, 3), (1, 2), (1, 3), (2, 3)]


class Steps:

    def __init__(self, eng, sem):
        self.eng, self.sem, self.n, self.count = eng, sem, 0, 0

    def done(self, ins):
        ins.then_inc(self.sem, 1)
        self.n, self.count = self.n + 1, self.count + 1
        self.eng.wait_ge(self.sem, self.n)

    @contextmanager
    def loop(self, lo, hi, per):
        start, count = self.n, self.count
        with self.eng.Fori(lo, hi) as i:
            self.n = start + (i - lo) * per
            yield i
            assert self.count - count == per, (self.count - count, per)
        self.n, self.count = start + (hi - lo) * per, count + (hi - lo) * per


def bucket_rows():
    dist = (T - 1) - np.arange(BW)
    n = np.maximum(dist, 0)
    exact = NBUCKET // 2
    nf = np.maximum(n, 1).astype(np.float32)
    large = exact + (np.log(nf / np.float32(exact)) / np.float32(np.log(MAXDIST / exact))
                     * np.float32(NBUCKET - exact)).astype(np.int32)
    b = np.where(n < exact, n, np.minimum(large, NBUCKET - 1))
    b = np.where(dist < 0, NBUCKET, b)
    return (np.arange(NBUCKET + 1)[:, None] == b[None, :]).astype(np.float32)


def build(nc, a, out, scratch):
    ctx = ExitStack()
    top = [4352]

    def at(name, shape, dt=F32, offset=None):
        size = -(-int(np.prod(shape[1:])) * 4 // 32) * 32
        if offset is None:
            offset = top[0]
            top[0] += size
        return nc.alloc_sbuf_tensor_at(name, shape, dt, offset=offset)

    KB = 1024
    raw = at("raw", [P, SLOTS, UK, NB])
    wsp = at("wsp", [P, SLOTS, UK, 2, NB], F32R)
    xs = at("xs", [P, KT, 2, T], F32R)
    arena_h = top[0]
    hs = at("hs", [P, KT, 2, T], F32R)
    xres = at("xres", [P, KT, T])
    arena_z = top[0]
    mixs = at("mixs", [P, KT, 2, T], F32R)
    arena_g = top[0]
    ycs = at("ycs", [P, LKT, 2, T], F32R)
    lat = at("lat", [P, LKT, T])
    arena_m = top[0]
    mn = at("mn", [P, LKT, T])
    xtok = at("xtok", [P, TT, D], offset=arena_z)
    vtok = at("vtok", [P, TT, VALW], offset=arena_z)
    kT = at("kT", [P, 8, T], offset=arena_z + 16 * KB)
    qT = at("qT", [P, 8, T], offset=arena_z + 24 * KB)
    osb = at("osb", [P, KT, T], offset=arena_g)
    bias_rows = at("bias_rows", [P, AH, BW], offset=arena_h)
    wgs = at("wgs", [P, KT, 2, P], F32R, offset=arena_h + 12 * KB)
    keys_dec = at("keys_dec", [P, 2, 2, 6, CHUNK], offset=arena_h + 12 * KB)
    scores_sb = at("scores_sb", [P, 2, 2, T], offset=arena_h + 18 * KB)
    osq = at("osq", [P, 4, T], offset=arena_h + 22 * KB)
    wg_raw = at("wg_raw", [P, KT, RANK], offset=arena_h + 28 * KB)
    q2 = at("q2", [P, AH, T], offset=arena_z)
    k2 = at("k2", [P, AH, T], offset=arena_z + 8 * KB)
    v2 = at("v2", [P, TT, AH * AD], offset=arena_z + 16 * KB)
    skew = at("skew", [P, AH, T], offset=arena_z + 24 * KB)
    xc, cc = lat, mn
    attn = at("attn", [P, BW], offset=arena_g)
    attnT = at("attnT", [P, BW], offset=arena_g + 3 * KB // 2)
    gate_a = at("gate_a", [P, 2, T], offset=arena_g + 3 * KB)
    gate_x = at("gate_x", [P, 2, T], offset=arena_g + 5 * KB)
    lru_t = at("lru_t", [P, 2, T], offset=arena_g + 7 * KB)
    lru_a = at("lru_a", [P, 2, T], offset=arena_g + 9 * KB)
    lru_u = at("lru_u", [P, 2, T], offset=arena_g + 11 * KB)
    wax = at("wax", [P, 2, LKT, P], offset=arena_h + 16 * KB)
    ytok = at("ytok", [P, TT, D], offset=arena_z)

    corr = at("corr", [P, 2, 2, T])
    z = at("z", [P, 2, T])
    h = at("h", [P, 2, T])
    fo = at("fo", [P, 2, T])
    xpad = at("xpad", [P, 2, T + CONV - 1])
    sq = at("sq", [P, 2, 2, T])
    ssq = at("ssq", [P, 2, 2, T])
    rstd = at("rstd", [P, T])
    rres = at("rres", [P, T])
    rtmp = at("rtmp", [P, T])
    rcol = at("rcol", [P, TT])
    par = at("par", [P, 2 * P])
    stage = at("stage", [P, 2, P], offset=arena_g + 13 * KB)
    ident = at("ident", [P, P])
    ones = at("ones", [P, P])
    cst = at("cst", [P, 2])
    gmix = at("gmix", [P, KT])
    c8 = at("c8", [P, LKT])
    lam_t = at("lam_t", [P, 3, LKT])
    segm = at("segm", [P, LKT, T], offset=arena_g)
    dec = at("dec", [P, 6, LKT])
    btot = at("btot", [P, NCH, LKT])
    glow = at("glow", [RANK, T], offset=arena_g + 12 * KB)
    wgu = at("wgu", [RANK, KEYW], offset=arena_g + 8 * KB)
    onehot = at("onehot", [NBUCKET + 1, BW], offset=arena_h + 30 * KB)
    table = at("table", [NBUCKET + 1, AH])
    tbc = at("tbc", [NBUCKET + 1, AH, P], offset=arena_h + 24 * KB)
    amax = at("amax", [P, 2])
    asum = at("asum", [P, 2])
    ainv = at("ainv", [P, 2])
    assert top[0] <= 229344, top[0]

    def psum(name, shape):
        return ctx.enter_context(nc.psum_tensor(name, shape, F32))

    acc = psum("acc", [P, 2, 2, 2, T])
    flat = [psum(f"misc{i}", [P, 2 * T]) for i in range(4)]
    M = [m[:].rearrange("p (a b) -> p a b", a=2) for m in flat]

    def sem(name):
        return ctx.enter_context(nc.semaphore(name))

    raw_landed = [sem(f"raw_landed{i}") for i in range(SLOTS)]
    hi_done, lo_done, unit_used = sem("hi_done"), sem("lo_done"), sem("unit_used")
    corr_ready, main_read = sem("corr_ready"), sem("main_read")
    value_ready, hi_ready, split_done = sem("value_ready"), sem("hi_ready"), sem("split_done")
    f_in, f_out = sem("f_in"), sem("f_out")
    sq_ready, ssq_done, norm_mm = sem("sq_ready"), sem("ssq_done"), sem("norm_mm")
    std_done, rstd_done, ssq_clear = sem("std_done"), sem("rstd_done"), sem("ssq_clear")
    x_landed = [sem(f"x_landed{q}") for q in range(4)]
    par_landed, wg_landed, tab_landed = sem("par_landed"), sem("wg_landed"), sem("tab_landed")
    const_done, zero_done, table_ready = sem("const_done"), sem("zero_done"), sem("table_ready")
    gain_landed, par_mm, par_done, x_mm = sem("gain_landed"), sem("par_mm"), sem("par_done"), sem("x_mm")
    bias_mm, bias_copied, bias_out, skew_landed = (sem("bias_mm"), sem("bias_copied"),
                                                   sem("bias_out"), sem("skew_landed"))
    bias_free = sem("bias_free")
    wg_hi, wg_ready, glow_mm, glow_corr, glow_done = (sem("wg_hi"), sem("wg_ready"), sem("glow_mm"),
                                                      sem("glow_corr"), sem("glow_done"))
    gate_mm, gate_abs, gate_min, gate_ln = (sem("gate_mm"), sem("gate_abs"), sem("gate_min"),
                                            sem("gate_ln"))
    rcol_mm, rcol_done = sem("rcol_mm"), sem("rcol_done")
    suffix_done, suffix_exp, dec_diff, dec_done = (sem("suffix_done"), sem("suffix_exp"),
                                                   sem("dec_diff"), sem("dec_done"))
    kd_ready, sc_mm, sc_copied, o_mm, o_copied = (sem("kd_ready"), sem("sc_mm"), sem("sc_copied"),
                                                  sem("o_mm"), sem("o_copied"))
    osum_done, onorm_mm, ostd_done = sem("osum_done"), sem("onorm_mm"), sem("ostd_done")
    qk_mm, attn_max, attn_exp, attn_ready = (sem("qk_mm"), sem("attn_max"), sem("attn_exp"),
                                             sem("attn_ready"))
    at_mm, at_copied, pv_mm, ya_hi, ya_done = (sem("at_mm"), sem("at_copied"), sem("pv_mm"),
                                               sem("ya_hi"), sem("ya_done"))
    qkv_ready, xc_ready, wax_landed = sem("qkv_ready"), sem("xc_ready"), sem("wax_landed")
    ga_mm, gx_mm, ga_act, gx_act = sem("ga_mm"), sem("gx_mm"), sem("ga_act"), sem("gx_act")
    lru_v, lru_s, lru_done, lam_in, lam_out = (sem("lru_v"), sem("lru_s"), sem("lru_done"),
                                               sem("lam_in"), sem("lam_out"))
    y_mm, y_copied, y_scaled, out_done = sem("y_mm"), sem("y_copied"), sem("y_scaled"), sem("out_done")
    act_steps, dve_steps, pool_steps = sem("act_steps"), sem("dve_steps"), sem("pool_steps")

    def prm(name, j=0, n=1):
        r = ROWS[name][0] + j
        return par[:, bass.ds(r, n)] if not isinstance(r, int) else par[:, r:r + n]

    def bc(ap, n=2):
        return ap[:].unsqueeze(1).to_broadcast([P, n, T])

    def kt_of(t, k):
        return t[:, k] if isinstance(k, int) else t[:, bass.ds(k, 1)].squeeze(1)

    def pair(t, i):
        return t[:, bass.ds(2 * i, 2)] if not isinstance(i, int) else t[:, 2 * i:2 * i + 2]

    LAST = BLOCK0["m2"] + 63

    def mlp_walk(loop, name, up, down):
        b0, r0 = BLOCK0[name], ROUND0[name]

        def go(fn, c, p, **kw):
            half = 0 if fn is up else 8
            for g in range(2):
                i = 2 * p + g
                fn(c, i, b0 + 16 * c + half + i, r0 + 16 * c + half + i, g, **kw)

        go(up, 0, 0, first=True)
        with loop(1, 4, "up") as p:
            go(up, 0, p)
        with loop(0, 4, "down") as p:
            go(down, 0, p)
        with loop(1, NCK - 1, "chunk") as c:
            with loop(0, 4, "up") as p:
                go(up, c, p)
            with loop(0, 4, "down") as p:
                go(down, c, p)
        with loop(0, 4, "up") as p:
            go(up, NCK - 1, p)
        go(down, NCK - 1, 0, last=True)
        with loop(1, 3, "last") as p:
            go(down, NCK - 1, p, last=True)
        go(down, NCK - 1, 3, last=True)

    def straight_walk(names, fn):
        for name in names:
            n = next(k for s, k, _ in STREAM if s == name)
            for i in range(n):
                fn(name, i, BLOCK0[name] + i, ROUND0[name] + i, i % 2)

    def mix_walk(loop, fn):
        b0, r0 = BLOCK0["mix"], ROUND0["mix"]
        with loop(1, 5, "mix") as m:
            u = 0
            for s in range(2):
                for j, units in enumerate(MIX_UNITS):
                    g = (6 * s + j) % 2
                    fn(j, 2 * m + (s - 2), b0 + 12 * m + (6 * s + j - 12), r0 - 9 + 9 * m, u, units, g)
                    u += units

    def units_of(round_, first, n):
        return [(round_ + (first + k) // SLOTS, (first + k) % SLOTS) for k in range(n)]

    GLA_A = ["gk", "gv", "gq", "gr"]
    L2_A = ["q", "k", "v", "xr", "scc", "scx", "br", "scb"]

    w_cols = {"gk": ("gla_w_in", KEYW), "gv": ("gla_w_in", 2 * KEYW), "gq": ("gla_w_in", 0),
              "gr": ("gla_w_in", 2 * KEYW + VALW), "go": ("gla_w_out", 0),
              "q": ("w_in_2", 0), "k": ("w_in_2", 1024), "v": ("w_in_2", 2048),
              "xr": ("w_in_2", 3072), "br": ("w_in_2", 4096), "scb": ("w_in_2", 5120),
              "scc": ("w_in_2", 6144), "scx": ("w_in_2", 7168), "lo": ("w_out_2", 0)}

    block = ctx.enter_context(nc.Block())

    @block.sync
    def _(sp):
        def load(w, row, col, rnd, slot, free=False):
            src = w[bass.ds(row, UK * P), bass.ds(col, NB)].rearrange("(t p) n -> p t n", p=P)
            if not free and not (isinstance(rnd, int) and rnd == 0):
                sp.wait_ge(lo_done, SLOTS * (rnd - 1) + slot + 1)
            sp.dma_start(raw[:, slot], src).then_inc(raw_landed[slot], 16)

        def loop(lo, hi, _):
            return sp.Fori(lo, hi)

        def block_load(w, col, rnd):
            for u in range(4):
                load(w, UK * P * u, col, rnd, u)

        for q in range(4):
            cols = slice(q * UK * P, (q + 1) * UK * P)
            sp.dma_start(xtok[:, :, cols], a["x"][:, cols].rearrange("(j p) n -> p j n", p=P)).then_inc(x_landed[q], 16)
        block_load(a["gla_w_in"], KEYW, 0)
        sp.dma_start(wg_raw[:], a["gla_w_in"][:, 2 * KEYW + 2 * VALW:].rearrange("(t p) n -> p t n", p=P)
                     ).then_inc(wg_landed, 16)
        sp.dma_start(wgu[:], a["gla_w_gate_up"]).then_inc(wg_landed, 16)
        for name, (r, k) in list(ROWS.items())[1:]:
            sp.dma_start(stage[r % P:r % P + k, r // P], a[name].rearrange("(r p) -> r p", p=P)).then_inc(par_landed, 16)

        def straight(name, i, b, rnd, g):
            if (name, i) == ("gk", 0):
                return
            w, col = w_cols[name]
            block_load(a[w], col + i * NB, rnd)

        straight_walk(GLA_A + ["go"], straight)

        def up(c, i, b, rnd, g, first=False):
            block_load(w_up[0], c * D + i * NB, rnd)

        def down(c, i, b, rnd, g, last=False):
            for u in range(4):
                load(w_up[1], c * D + UK * P * u, i * NB, rnd, u)

        w_up = (a["mlp_w_up"], a["mlp_w_down"])
        mlp_walk(loop, "m1", up, down)
        sp.wait_ge(bias_out, 16)
        sp.wait_ge(o_mm, HEADS)
        for hd in range(AH):
            src = scratch[hd * P * BW + P - 1:hd * P * BW + P - 1 + P * (BW - 1)]
            sp.dma_start(skew[:, hd], src.rearrange("(p n) -> p n", n=BW - 1)[:, 0:T]).then_inc(skew_landed, 16)

        def straight2(name, i, b, rnd, g):
            w, col = w_cols[name]
            block_load(a[w], col + i * NB, rnd)
            if (name, i) == ("k", 0):
                sp.wait_ge(unit_used, SLOTS * ROUND0["q"])
                for k, g in enumerate(("lru_wa_2", "lru_wx_2")):
                    sp.dma_start(wax[:, k], a[g].rearrange("g p n -> p g n")).then_inc(wax_landed, 16)

        straight_walk(L2_A, straight2)

        def mix(j, n, b, rnd, first, units, g):
            slots = units_of(rnd, first, units)
            if j % 2 == 0:
                for k, (r, s) in enumerate(slots):
                    load(a["w_in_2"], UK * P * k, 8192 + (j // 2) * D + n * NB, r, s)
            else:
                w = a[("w_attn_o_2", "w_lru_o_2", "w_sc_o_2")[j // 2]]
                load(w, UK * P, n * NB, *slots[1])
                load(w, 0, n * NB, *slots[0], free=True)

        mix_walk(loop, mix)
        straight_walk(["lo"], straight2)
        w_up = (a["w_mlp_up_2"], a["w_mlp_down_2"])
        mlp_walk(loop, "m2", up, down)
        for j in range(TT):
            for half in range(2):
                sp.wait_ge(y_scaled, 2 * j + half + 1)
                sp.dma_start(out[j * P:(j + 1) * P, half * 1024:half * 1024 + 1024],
                             ytok[:, j, half * 1024:half * 1024 + 1024]).then_inc(out_done, 16)
        sp.wait_ge(out_done, 64)

    @block.gpsimd
    def _(pool):
        own = Steps(pool, pool_steps)
        own.done(pool.memset(ident[:], 0.0))
        pool.affine_select(out=ident[:], in_=ident[:], compare_op=ALU.not_equal, fill=1.0, base=0,
                           pattern=[[-1, P]], channel_multiplier=1).then_inc(const_done, 1)
        pool.memset(ones[:], 1.0).then_inc(const_done, 1)
        pool.memset(cst[:, 0:1], EPS).then_inc(const_done, 1)
        pool.memset(cst[:, 1:2], 1.0).then_inc(const_done, 1)
        for norm in range(5):
            two = norm == 2
            if norm:
                pool.wait_ge(norm_mm, norm)
            own.done(pool.memset(ssq[:], 0.0))
            with pool.Fori(0, PAIRS) as i:
                pool.wait_ge(sq_ready, 8 * norm + i + 1)
                if norm:
                    pool.wait_ge(ssq_done, 8 * norm + i)
                else:
                    pool.wait_ge(ssq_done, i)
                for k in range(1 + two):
                    ins = pool.tensor_tensor(ssq[:, k], ssq[:, k], sq[:, k], ALU.add)
                ins.then_inc(ssq_done, 1)
            if norm == 0:
                pool.memset(wgs[:].bitcast(F32), 0.0).then_inc(zero_done, 1)
                own.done(pool.memset(table[:], NEG))
                pool.memset(xpad[:], 0.0).then_inc(zero_done, 1)
                own.done(pool.memset(segm[:], 1.0))
                first = segm[:].rearrange("p k (c s) -> p k c s", s=CHUNK)[:, :, :, 0:1]
                pool.memset(first, 0.0).then_inc(zero_done, 1)

    @block.tensor
    def _(pe):
        def loop(lo, hi, _):
            return pe.Fori(lo, hi)

        def gemm(b, units, g, x, ready, k0=0, tokens_out=False, mid=None, before=None, mid_unit=2):
            if not (isinstance(b, int) and b < 2):
                pe.wait_ge(main_read, b - 1)
            for u, (rnd, slot) in enumerate(units):
                if before:
                    before(u)
                pe.wait_ge(lo_done, SLOTS * rnd + slot + 1)
                for s, v in ready(u):
                    pe.wait_ge(s, v)
                for t in range(UK):
                    k = UK * u + t
                    start, stop = k == 0, (u == len(units) - 1 and t == UK - 1)
                    for j in range(2):
                        cols = slice(j * P, j * P + P)
                        if tokens_out:
                            pe.matmul(acc[:, g, j], x[:, k0 + k, 0, cols], wsp[:, slot, t], start=start,
                                      stop=False, skip_group_check=True)
                            ins = pe.matmul(acc[:, g, j, 1], x[:, k0 + k, 1, cols], wsp[:, slot, t, 0],
                                            start=False, stop=stop, skip_group_check=True)
                        else:
                            pe.matmul(acc[:, g, j], wsp[:, slot, t, 0, cols], x[:, k0 + k], start=start,
                                      stop=False, skip_group_check=True)
                            ins = pe.matmul(acc[:, g, j, 1], wsp[:, slot, t, 1, cols], x[:, k0 + k, 0],
                                            start=False, stop=stop, skip_group_check=True)
                ins.then_inc(unit_used, 1)
                if mid and u == mid_unit:
                    mid()

        def norm(n, two=False):
            def run():
                pe.wait_ge(ssq_done, 8 * (n + 1))
                for s, v in {0: [], 1: [(ostd_done, HEADS)], 2: [(std_done, 2)], 3: [(gx_act, 4)]}[n]:
                    pe.wait_ge(s, v)
                for k in range(1 + two):
                    for j in range(2):
                        ins = pe.matmul(M[0][:, k], ones[:], ssq[:, k, j], start=(j == 0), stop=(j == 1),
                                        skip_group_check=True)
                ins.then_inc(norm_mm, 1)
            return run

        def split_upto(base):
            return lambda u: [(split_done, base + 2 * (u + 1))]

        pe.wait_ge(const_done, 2)
        pe.wait_ge(gain_landed, 16)
        pe.transpose(M[3][:, 0, 0:KT], stage[0:KT, 0], ident[0:KT, 0:KT]).then_inc(par_mm, 1)

        def inputs(u):
            for i in ((0, 1, 2, 3, 4), (5, 6), (7,), ())[u]:
                if i % 2 == 0:
                    pe.wait_ge(x_landed[i // 2], 16)
                if i >= 3:
                    pe.wait_ge(value_ready, i - 2)
                for t in range(2):
                    for j in range(TT):
                        k = 2 * i + t
                        ins = pe.transpose(M[i % 3][:, t, j * P:(j + 1) * P], xtok[:, j, k * P:(k + 1) * P], ident[:])
                ins.then_inc(x_mm, 1)
            if u == 3:
                pe.wait_ge(par_landed, 16 * (len(ROWS) - 1))
                pe.wait_ge(par_done, 1)
                pe.transpose(M[3][:, 0, 0:ROWS_A], stage[0:ROWS_A, 0], ident[0:ROWS_A, 0:ROWS_A])
                pe.transpose(M[3][:, 1, 0:ROWS_B], stage[0:ROWS_B, 1], ident[0:ROWS_B, 0:ROWS_B]).then_inc(par_mm, 1)

        def hooks(name, i):
            if name == "gv":
                pe.wait_ge(table_ready, 1)
                if i:
                    pe.wait_ge(bias_copied, i)
                else:
                    pe.wait_ge(gate_min, 2)
                    pe.wait_ge(gate_abs, 2)
                pe.matmul(flat[3][:, 0:BW], tbc[:, i], onehot[:], start=True, stop=True).then_inc(bias_mm, 1)
            if (name, i) == ("gk", 1):
                pe.wait_ge(wg_ready, 1)
                pe.wait_ge(std_done, 1)
                for k in range(KT):
                    pe.matmul(M[1], wgs[:, k, 0], xs[:, k], start=(k == 0), stop=False, skip_group_check=True)
                    ins = pe.matmul(M[1][:, 1], wgs[:, k, 1], xs[:, k, 0], start=False, stop=(k == KT - 1),
                                    skip_group_check=True)
                ins.then_inc(glow_mm, 1)
                pe.wait_ge(rstd_done, 1)
                for j in range(TT):
                    ins = pe.transpose(M[2][:, j, 0:P], rstd[:, j * P:(j + 1) * P], ident[:])
                ins.then_inc(rcol_mm, 1)
            if name == "gk" and i in (2, 3):
                pe.wait_ge(glow_done, 1)
                pe.wait_ge(rcol_done, 1)
                pe.wait_ge(par_done, 2)
                if i == 3:
                    pe.wait_ge(gate_min, 1)
                    pe.wait_ge(gate_abs, 1)
                for f in range(4):
                    ft = 4 * (i - 2) + f
                    ins = pe.matmul(M[2 + f // 2][:, f % 2], wgu[:, ft * P:(ft + 1) * P], glow[:],
                                    start=True, stop=True, skip_group_check=True)
                ins.then_inc(gate_mm, 1)
            step = {"gq": i, "gr": 4 + i}.get(name, 99)
            if 1 <= step <= 4:
                hd = step - 1
                pe.wait_ge(kd_ready, hd + 1)
                if hd:
                    pe.wait_ge(sc_copied, hd)
                for cs in range(NCH):
                    rows = slice((cs % 2) * CHUNK, (cs % 2) * CHUNK + CHUNK)
                    for ct in range(cs, NCH):
                        for dt in range(2):
                            if ct == cs:
                                keys = kT[:, 2 * hd + dt, cs * CHUNK:(cs + 1) * CHUNK]
                            else:
                                keys = keys_dec[:, hd % 2, dt, CHUNK_PAIRS.index((cs, ct))]
                            ins = pe.matmul(M[1][rows, cs // 2, ct * CHUNK:(ct + 1) * CHUNK], keys,
                                            qT[:, 2 * hd + dt, ct * CHUNK:(ct + 1) * CHUNK],
                                            start=(dt == 0), stop=(dt == 1), skip_group_check=True)
                ins.then_inc(sc_mm, 1)
            if 2 <= step <= 5:
                hd = step - 2
                pe.wait_ge(sc_copied, hd + 1)
                pe.wait_ge(bias_copied, AH)
                if hd:
                    pe.wait_ge(o_copied, hd)
                for dv in range(4):
                    for ct in range(NCH):
                        cols = slice(ct * CHUNK, (ct + 1) * CHUNK)
                        parts = [(0, CHUNK if ct == 0 else P)] + ([(1, CHUNK if ct == 2 else P)] if ct > 1 else [])
                        for s, n in parts:
                            ins = pe.matmul(M[2 + dv // 2][:, dv % 2, cols],
                                            vtok[0:n, s, hd * DV + dv * P:hd * DV + (dv + 1) * P],
                                            scores_sb[0:n, hd % 2, s, cols], start=(s == 0),
                                            stop=(s == parts[-1][0]), skip_group_check=True)
                ins.then_inc(o_mm, 1)
            if 3 <= step <= 6:
                hd = step - 3
                pe.wait_ge(osum_done, hd + 1)
                if hd:
                    pe.wait_ge(ostd_done, hd)
                for j in range(2):
                    ins = pe.matmul(M[0][:, 0], ones[:], osq[:, j], start=(j == 0), stop=(j == 1),
                                    skip_group_check=True)
                ins.then_inc(onorm_mm, 1)

        def straight(name, i, b, rnd, g):
            mid, before = (norm(0), inputs) if (name, i) == ("gk", 0) else (None, None)
            gemm(b, units_of(rnd, 0, 4), g, xs, split_upto(PAIR0["x1"]), tokens_out=(name == "gv"), mid=mid,
                 before=before, mid_unit=3)
            hooks(name, i)

        straight_walk(GLA_A, straight)

        def out_proj(name, x, base):
            r0, b0 = ROUND0[name], BLOCK0[name]
            with pe.Fori(0, 4) as p:
                for g in range(2):
                    gemm(b0 + 2 * p + g, units_of(r0 + 2 * p + g, 0, 4), g, x, split_upto(base))

        out_proj("go", hs, PAIR0["gr"])

        def mlp(name, x_base, h_base, norm_no, final):
            def up(c, i, b, rnd, g, first=False):
                gemm(b, units_of(rnd, 0, 4), g, xs, split_upto(x_base),
                     mid=norm(norm_no) if first and g == 0 else None)

            def down(c, i, b, rnd, g, last=False):
                gemm(b, units_of(rnd, 0, 4), g, hs, split_upto(h_base + 8 * c))
                if last and final:
                    y_transpose(i)

            mlp_walk(loop, name, up, down)

        def y_transpose(i):
            if isinstance(i, int) and i == 0:
                return
            pe.wait_ge(value_ready, FINAL0 + i)
            if not (isinstance(i, int) and i == 1):
                pe.wait_ge(y_copied, i - 1)
            for t in range(2):
                for j in range(TT):
                    ins = pe.transpose(M[1][:, j, t * P:(t + 1) * P], h[:, t, j * P:(j + 1) * P], ident[:])
            ins.then_inc(y_mm, 1)

        mlp("m1", PAIR0["xm1"], PAIR0["h1"], 1, False)

        def hooks2(name, i):
            if (name, i) == ("k", 0):
                pe.wait_ge(rstd_done, 4)
                for j in range(TT):
                    ins = pe.transpose(M[2][:, j, 0:P], rstd[:, j * P:(j + 1) * P], ident[:])
                ins.then_inc(rcol_mm, 1)
            order = {"xr": 0, "scc": 4, "scx": 8, "br": 12}
            if name not in order:
                return
            s = order[name] + i
            if s < AH:
                pe.wait_ge(qkv_ready, 12)
                if s:
                    pe.wait_ge(attn_max, s)
                pe.matmul(flat[1][:, 0:P], q2[:, s, 0:P], k2[:, s, 0:P], start=True, stop=True, skip_group_check=True)
                pe.matmul(flat[1][:, P:BW], q2[:, s, P:T], k2[:, s, :], start=True, stop=True,
                          skip_group_check=True).then_inc(qk_mm, 1)
            if 1 <= s <= AH:
                pe.wait_ge(attn_ready, s)
                if s > 1:
                    pe.wait_ge(at_copied, s - 1)
                for n in range(3):
                    ins = pe.transpose(flat[2][:, n * P:(n + 1) * P], attn[:, n * P:(n + 1) * P], ident[:])
                ins.then_inc(at_mm, 1)
            if 2 <= s <= AH + 1:
                hd = s - 2
                pe.wait_ge(at_copied, hd + 1)
                if hd:
                    pe.wait_ge(ya_done, hd)
                pe.matmul(M[3][:, 0], v2[:, 0, hd * AD:(hd + 1) * AD], attnT[:, 0:T], start=True, stop=False,
                          skip_group_check=True)
                pe.matmul(M[3][:, 0, P:T], v2[:, 1, hd * AD:(hd + 1) * AD], attnT[:, T:BW], start=False,
                          stop=True, skip_group_check=True).then_inc(pv_mm, 1)
            if 4 <= s < 12:
                li, kind = (s - 4) // 2, (s - 4) % 2
                pe.wait_ge(xc_ready, li + 1)
                pe.wait_ge(wax_landed, 32)
                if kind:
                    pe.wait_ge(ga_act, li + 1)
                elif li:
                    pe.wait_ge(gx_act, li)
                for j in range(2):
                    ins = pe.matmul(M[0][:, j], wax[:, kind, 2 * li + j], xc[:, 2 * li + j], start=True, stop=True,
                                    skip_group_check=True)
                ins.then_inc(gx_mm if kind else ga_mm, 1)

        def straight2(name, i, b, rnd, g):
            mid = norm(2, two=True) if (name, i) == ("q", 0) else None
            gemm(b, units_of(rnd, 0, 4), g, xs, split_upto(PAIR0["x2"]), tokens_out=(name == "v"), mid=mid)
            hooks2(name, i)

        straight_walk(L2_A, straight2)

        def mix(j, n, b, rnd, first, units, g):
            if j % 2 == 0:
                gemm(b, units_of(rnd, first, units), g, xs, lambda u: [])
            else:
                x, k0 = ((hs, 0), (hs, LKT), (ycs, 0))[j // 2]
                gemm(b, units_of(rnd, first, units), g, x,
                     lambda u: [(split_done, PAIR0["mix"])] + ([(ya_done, AH)] if j == 1 else []), k0=k0)

        mix_walk(loop, mix)
        out_proj("lo", mixs, PAIR0["mix"])
        mlp("m2", PAIR0["xm2"], PAIR0["h2"], 3, True)
        y_transpose(PAIRS)
        pe.wait_ge(ssq_done, 40)
        for j in range(TT):
            for k in range(2):
                ins = pe.matmul(M[0][:, 0, 2 * j:2 * j + 2], ssq[:, 0, k, j * P:(j + 1) * P], ones[:, 0:2], start=(k == 0),
                                stop=(k == 1), skip_group_check=True)
        ins.then_inc(norm_mm, 1)


    def look_ahead(rnd, first, n):
        return units_of(rnd + 1, first, n)

    def is_past_end(rnd):
        return isinstance(rnd, int) and rnd >= ROUNDS

    @block.scalar
    def _(act):
        own = Steps(act, act_steps)
        PER = {"up": 0, "down": 0, "chunk": 0, "last": 0, "mix": 0}

        def loop(lo, hi, kind):
            return own.loop(lo, hi, PER[kind])

        def split_hi(rnd, slot):
            if is_past_end(rnd):
                return
            act.wait_ge(raw_landed[slot], 16 * (rnd + 1))
            if not (isinstance(rnd, int) and rnd == 0):
                act.wait_ge(unit_used, SLOTS * (rnd - 1) + slot + 1)
            act.activation(wsp[:, slot, :, 0], raw[:, slot], ACT.Copy).then_inc(hi_done, 1)

        def evac(b, rnd, first, n, g):
            ahead = look_ahead(rnd, first, n)
            for r, s in ahead[:-1]:
                split_hi(r, s)
            r, s = units_of(rnd, first, n)[-1]
            act.wait_ge(unit_used, SLOTS * r + s + 1)
            act.activation(corr[:, g], acc[:, g, :, 1], ACT.Copy).then_inc(corr_ready, 1)
            split_hi(*ahead[-1])

        def emit(pair_no, dst, i, src=h):
            act.wait_ge(value_ready, pair_no + 1)
            act.activation(pair(dst, i)[:, :, 0], src[:], ACT.Copy).then_inc(hi_ready, 1)

        def squares(n, i, gain=None):
            if not (n == 0 and isinstance(i, int) and i == 0):
                act.wait_ge(ssq_done, 8 * n + i)
            ins = act.activation(sq[:, 0], pair(xres, i), ACT.Square)
            if gain:
                for j in range(2):
                    ins = act.activation(sq[:, 1, j], kt_of(xres, 2 * i + j), ACT.Square, scale=prm(gain, 2 * i + j))
            ins.then_inc(sq_ready, 1)

        def function(no, func, biases=None):
            act.wait_ge(f_in, no + 1)
            if biases is None:
                act.activation(fo[:], z[:], func).then_inc(f_out, 1)
            else:
                for j in range(2):
                    ins = act.activation(fo[:, j], z[:, j], func, bias=biases[j])
                ins.then_inc(f_out, 1)

        def std(n):
            act.wait_ge(norm_mm, n + 1)
            act.activation(rtmp[:], M[0][:, 0], ACT.Sqrt, scale=1.0 / D, bias=cst[:, 0:1]).then_inc(std_done, 1)
            if n == 2:
                act.wait_ge(rstd_done, 3)
                act.activation(rtmp[:], rstd[:], ACT.Sqrt, scale=1.0 / D, bias=cst[:, 0:1]).then_inc(std_done, 1)

        act.dma_start(stage[0:KT, 0], a["gla_norm"].rearrange("(r p) -> r p", p=P)).then_inc(gain_landed, 16)
        for i in range(PAIRS):
            emit(PAIR0["x1"] + i, xs, i, src=(h, fo)[i % 2])
            squares(0, i)
            if i % 2 == 1:
                split_hi(0, i // 2)
        act.wait_ge(const_done, 4)

        def gla_hooks(name, i):
            if name == "gv":
                act.wait_ge(bias_mm, i + 1)
                act.activation(bias_rows[:, i], flat[3][:, 0:BW], ACT.Copy).then_inc(bias_copied, 1)
            if (name, i) == ("gq", 0):
                act.wait_ge(bias_copied, AH)
                act.dma_start(scratch.rearrange("(h p n) -> p h n", h=AH, p=P), bias_rows[:]).then_inc(bias_out, 16)
            if (name, i) == ("gk", 0):
                act.wait_ge(wg_landed, 32)
                act.wait_ge(zero_done, 1)
                act.activation(wgs[:, :, 0, 0:RANK], wg_raw[:], ACT.Copy).then_inc(wg_hi, 1)
            if (name, i) == ("gk", 1):
                act.wait_ge(glow_mm, 1)
                act.activation(fo[0:RANK, 0], M[1][0:RANK, 1], ACT.Copy).then_inc(glow_corr, 1)
                act.wait_ge(zero_done, 3)
                act.dma_start(table[0:NBUCKET], a["rel_table_2"]).then_inc(tab_landed, 16)
                act.dma_start(onehot[:], a["onehot"]).then_inc(tab_landed, 16)
            if name == "gk" and i in (2, 3):
                act.wait_ge(gate_mm, i - 1)
                for f in range(4):
                    ft = 4 * (i - 2) + f
                    ins = act.activation(lat[:, ft], M[2 + f // 2][:, f % 2], ACT.Abs, bias=prm("gla_b_gate", ft))
                ins.then_inc(gate_abs, 1)
            if (name, i) == ("gv", 4):
                own.done(act.activation(lam_t[:, 0], prm("lru_lambda_2", 0, LKT), ACT.Abs))
                act.activation(lam_t[:, 1], lam_t[:, 0], ACT.Exp, scale=-1.0).then_inc(lam_in, 1)
            if (name, i) == ("gv", 0):
                act.wait_ge(gate_abs, 2)
                own.done(act.activation(lat[:], lat[:], ACT.Exp, scale=-1.0))
                act.activation(lat[:], lat[:], ACT.Ln, bias=cst[:, 1:2]).then_inc(gate_ln, 1)
            if (name, i) == ("gv", 3):
                act.wait_ge(suffix_done, 1)
                act.activation(lat[:], lat[:], ACT.Exp, scale=1.0 / TEMP).then_inc(suffix_exp, 1)
                act.wait_ge(dec_diff, 1)
                act.activation(dec[:], dec[:], ACT.Exp, scale=1.0 / TEMP).then_inc(dec_done, 1)
            step = {"gq": i, "gr": 4 + i}.get(name, 99)
            if 1 <= step <= 4:
                hd = step - 1
                act.wait_ge(sc_mm, hd + 1)
                if hd >= 2:
                    act.wait_ge(o_mm, hd - 1)
                for rows, s, t0 in ((slice(0, 64), 0, 0), (slice(64, P), 0, 64), (slice(0, 64), 1, 128),
                                    (slice(64, P), 1, 192)):
                    ins = act.activation(scores_sb[rows, hd % 2, s, t0:T], M[1][rows, s, t0:T], ACT.Copy)
                ins.then_inc(sc_copied, 1)
            if 3 <= step <= 6:
                hd = step - 3
                act.wait_ge(onorm_mm, hd + 1)
                act.activation(rtmp[:], M[0][:, 0], ACT.Sqrt, scale=1.0 / DV, bias=cst[:, 0:1]).then_inc(ostd_done, 1)
            if 2 <= step <= 5:
                hd = step - 2
                act.wait_ge(o_mm, hd + 1)
                if hd:
                    act.wait_ge(onorm_mm, hd)
                for k in range(2):
                    act.activation(osb[:, 4 * hd + 2 * k:4 * hd + 2 * k + 2], M[2 + k], ACT.Copy)
                    ins = act.activation(osq[:, 2 * k:2 * k + 2], M[2 + k], ACT.Square)
                ins.then_inc(o_copied, 1)

        def gla(name, i, b, rnd, g):
            evac(b, rnd, 0, 4, g)
            if (name, i) == ("gk", 0):
                std(0)
            if name == "gr":
                function(FUN0["gr"] + i, ACT.Sigmoid)
                if i == 0:
                    act.wait_ge(bias_out, 16)
                emit(PAIR0["gr"] + i, hs, i)
            gla_hooks(name, i)

        straight_walk(GLA_A, gla)

        def out_proj(name, pairs0, norm_no):
            with own.loop(0, 4, 0) as p:
                for g in range(2):
                    i = 2 * p + g
                    evac(BLOCK0[name] + i, ROUND0[name] + i, 0, 4, g)
                    emit(pairs0 + i, xs, i)
                    squares(norm_no, i)

        out_proj("go", PAIR0["xm1"], 1)

        def mlp(name, h_base, norm_no, then):
            def up(c, i, b, rnd, g, first=False):
                evac(b, rnd, 0, 4, g)
                if first and g == 0:
                    std(norm_no)
                emit(h_base + 8 * c + i, hs, i, src=z)

            def down(c, i, b, rnd, g, last=False):
                evac(b, rnd, 0, 4, g)
                if last:
                    then(i)

            mlp_walk(loop, name, up, down)

        def to_second(i):
            emit(PAIR0["x2"] + i, xs, i)
            squares(2, i, gain="final_norm")

        mlp("m1", PAIR0["h1"], 1, to_second)

        def l2_hooks(name, i):
            order = {"xr": 0, "scc": 4, "scx": 8, "br": 12}
            if name not in order:
                return
            s = order[name] + i
            if s < AH:
                act.wait_ge(attn_max, s + 1)
                act.activation(attn[:, 0:P], attn[:, 0:P], ACT.Exp, bias=amax[:, 0:1], accum_out=asum[:, 0:1])
                act.activation(attn[:, P:BW], attn[:, P:BW], ACT.Exp, bias=amax[:, 1:2],
                               accum_out=asum[:, 1:2]).then_inc(attn_exp, 1)
            if 1 <= s <= AH:
                act.wait_ge(at_mm, s)
                if s > 1:
                    act.wait_ge(pv_mm, s - 1)
                act.activation(attnT[:], flat[2][:, 0:BW], ACT.Copy).then_inc(at_copied, 1)
            if 2 <= s <= AH + 1:
                act.wait_ge(pv_mm, s - 1)
                act.activation(hs[:, s - 2, 0], M[3][:, 0], ACT.Copy).then_inc(ya_hi, 1)
            if 6 <= s <= 12 and s % 2 == 0:
                li = (s - 6) // 2
                act.wait_ge(lru_s, li + 1)
                act.activation(lru_u[:], lru_t[:], ACT.Sqrt, scale=-1.0).then_inc(lru_v, 1)
            if 4 <= s < 12:
                li, kind = (s - 4) // 2, (s - 4) % 2
                if kind == 0:
                    act.wait_ge(ga_mm, li + 1)
                    for j in range(2):
                        ins = act.activation(gate_a[:, j], M[0][:, j], ACT.Sigmoid, bias=prm("lru_ba_2", 2 * li + j))
                    ins.then_inc(ga_act, 1)
                else:
                    act.wait_ge(gx_mm, li + 1)
                    if li:
                        act.wait_ge(lru_done, li)
                    for j in range(2):
                        ins = act.activation(gate_x[:, j], M[0][:, j], ACT.Sigmoid, bias=prm("lru_bx_2", 2 * li + j))
                    ins.then_inc(gx_act, 1)
                    act.wait_ge(ga_act, li + 1)
                    act.wait_ge(lam_out, 1)
                    for j in range(2):
                        c = c8[:, 2 * li + j:2 * li + j + 1]
                        act.activation(lru_t[:, j], gate_a[:, j], ACT.Tanh, scale=c)
                        ins = act.activation(lru_a[:, j], gate_a[:, j], ACT.Exp, scale=c)
                    own.done(ins)
                    act.activation(gate_a[:], lru_a[:], ACT.Square).then_inc(lru_v, 1)

        def second(name, i, b, rnd, g):
            evac(b, rnd, 0, 4, g)
            if (name, i) == ("q", 0):
                std(2)
            if name == "br":
                function(FUN0["br"] + i, ACT.Gelu_apprx_tanh)
                emit(PAIR0["yb"] + i, hs, 4 + i)
            if name == "scb":
                emit(PAIR0["yc"] + i, ycs, i)
            l2_hooks(name, i)

        straight_walk(L2_A, second)

        def mix(j, n, b, rnd, first, units, g):
            evac(b, rnd, first, units, g)
            if j % 2 == 0:
                function(FUN0["gate"] + 3 * n + j // 2, ACT.Sigmoid,
                         [prm("gate_b_2", (j // 2) * KT + 2 * n + k) for k in range(2)])
            if j == 5:
                emit(PAIR0["mix"] + n, mixs, n)

        mix_walk(loop, mix)
        out_proj("lo", PAIR0["xm2"], 3)

        def y_copy(i):
            if isinstance(i, int) and i == 0:
                return
            act.wait_ge(y_mm, i)
            act.activation(ytok[:, :, bass.ds(NB * (i - 1), NB)], M[1], ACT.Copy).then_inc(y_copied, 1)

        def to_output(i):
            act.wait_ge(value_ready, FINAL0 + i + 1)
            squares(4, i)
            y_copy(i)

        mlp("m2", PAIR0["h2"], 3, to_output)
        y_copy(PAIRS)
        act.wait_ge(norm_mm, 5)
        act.activation(rcol[:], M[0][:, 0, 0:4:2], ACT.Sqrt, scale=1.0 / D, bias=cst[:, 0:1]).then_inc(std_done, 1)

    @block.vector
    def _(dve):
        own = Steps(dve, dve_steps)
        UP, DOWN, LASTD, MIX = 2, 2, 2, 8
        PER = {"up": UP, "down": DOWN, "chunk": 4 * UP + 4 * DOWN, "last": LASTD, "mix": MIX}

        def loop(lo, hi, kind):
            return own.loop(lo, hi, PER[kind])

        def split_lo(rnd, slot):
            if is_past_end(rnd):
                return
            dve.wait_ge(hi_done, SLOTS * rnd + slot + 1)
            dve.tensor_tensor(wsp[:, slot, :, 1], raw[:, slot], wsp[:, slot, :, 0].bitcast(F32),
                              ALU.subtract).then_inc(lo_done, 1)

        def take(b, rnd, first, n, g):
            for r, s in look_ahead(rnd, first, n)[:-1]:
                split_lo(r, s)
            dve.wait_ge(corr_ready, b + 1)
            dve.tensor_tensor(z[:], acc[:, g, :, 0], corr[:, g], ALU.add).then_inc(main_read, 1)
            dve.wait_ge(main_read, b + 1)

        def last_split(rnd, first, n):
            split_lo(*look_ahead(rnd, first, n)[-1])

        def emit(pair_no, dst, i, src=h):
            dve.wait_ge(hi_ready, pair_no + 1)
            dve.tensor_tensor(pair(dst, i)[:, :, 1], src[:], pair(dst, i)[:, :, 0].bitcast(F32),
                              ALU.subtract).then_inc(split_done, 1)
            dve.wait_ge(split_done, pair_no + 1)

        def gained(i, gain):
            for j in range(2):
                g = gmix[:, bass.ds(2 * i + j, 1)] if gain == "gmix" else prm(gain, 2 * i + j)
                ins = dve.tensor_scalar(h[:, j], kt_of(xres, 2 * i + j), g, None, ALU.mult)
            ins.then_inc(value_ready, 1)

        def scaled(dst, factor=1.0):
            return dve.scalar_tensor_tensor(out=dst, in0=z[:], scalar=factor, in1=bc(rstd), op0=ALU.mult, op1=ALU.mult)

        dve.wait_ge(par_mm, 1)
        dve.tensor_copy(par[:, 0:KT], M[3][:, 0, 0:KT]).then_inc(par_done, 1)
        dve.wait_ge(par_done, 1)
        for i in range(PAIRS + 1):
            if i < PAIRS:
                dve.wait_ge(x_mm, i + 1)
                dve.tensor_copy(xres[:, 2 * i:2 * i + 2], M[i % 3])
                for j in range(2):
                    ins = dve.tensor_scalar((h, fo)[i % 2][:, j], M[i % 3][:, j], prm("gla_norm", 2 * i + j), None, ALU.mult)
                ins.then_inc(value_ready, 1)
            if i:
                emit(PAIR0["x1"] + i - 1, xs, i - 1, src=(h, fo)[(i - 1) % 2])
            if i and i % 2 == 0:
                split_lo(0, i // 2 - 1)

        def parameters():
            dve.wait_ge(par_mm, 2)
            dve.tensor_copy(par[:, KT:ROWS_A], M[3][:, 0, KT:ROWS_A])
            dve.tensor_copy(par[:, P:P + ROWS_B], M[3][:, 1, 0:ROWS_B]).then_inc(par_done, 1)
            dve.wait_ge(par_done, 2)
            dve.tensor_tensor(gmix[:], prm("final_norm", 0, KT), prm("norm_mix_g_2", 0, KT), ALU.mult)
            own.done(dve.tensor_scalar(lam_t[:, 2], prm("lru_lambda_2", 0, LKT), -1.0, 0.0, ALU.mult, ALU.max))

        def softplus():
            dve.wait_ge(lam_in, 1)
            e, s1, s2 = lam_t[:, 1], lam_t[:, 0], c8[:]
            own.done(dve.tensor_scalar(s1, e, 2.0, None, ALU.add))
            own.done(dve.reciprocal(s1, s1))
            own.done(dve.tensor_tensor(s1, s1, e, ALU.mult))
            own.done(dve.tensor_tensor(s2, s1, s1, ALU.mult))
            own.done(dve.tensor_scalar(e, s2, 1.0 / 15, 1.0 / 13, ALU.mult, ALU.add))
            for k in (11, 9, 7, 5, 3, 1):
                own.done(dve.tensor_tensor(e, e, s2, ALU.mult))
                own.done(dve.tensor_scalar(e, e, 1.0 / k, None, ALU.add))
            own.done(dve.tensor_tensor(e, e, s1, ALU.mult))
            own.done(dve.scalar_tensor_tensor(out=e, in0=e, scalar=2.0, in1=lam_t[:, 2], op0=ALU.mult, op1=ALU.add))
            dve.tensor_scalar(c8[:], e, -8.0, None, ALU.mult).then_inc(lam_out, 1)

        def gla_hooks(name, i):
            if (name, i) == ("gv", 5):
                softplus()
            if (name, i) == ("gk", 0):
                parameters()
                dve.wait_ge(wg_hi, 1)
                dve.tensor_tensor(wgs[:, :, 1, 0:RANK], wg_raw[:], wgs[:, :, 0, 0:RANK].bitcast(F32),
                                  ALU.subtract).then_inc(wg_ready, 1)
            if (name, i) == ("gk", 1):
                dve.wait_ge(glow_corr, 1)
                own.done(dve.tensor_tensor(glow[:], M[1][0:RANK, 0], fo[0:RANK, 0], ALU.add))
                dve.tensor_tensor(glow[:], glow[:], rstd[0:RANK], ALU.mult).then_inc(glow_done, 1)
                dve.wait_ge(rcol_mm, 1)
                dve.tensor_copy(rcol[:], M[2][:, :, 0]).then_inc(rcol_done, 1)
                dve.wait_ge(tab_landed, 32)
                dve.wait_ge(glow_mm, 1)
                for hd in range(AH):
                    ins = dve.tensor_copy(tbc[:, hd], table[:, hd:hd + 1].to_broadcast([NBUCKET + 1, P]))
                ins.then_inc(table_ready, 1)
            if name == "gk" and i in (2, 3):
                dve.wait_ge(gate_abs, i - 1)
                for f in range(4):
                    ft = 4 * (i - 2) + f
                    ins = dve.tensor_scalar(mn[:, ft], M[2 + f // 2][:, f % 2], prm("gla_b_gate", ft), 0.0, ALU.add, ALU.min)
                ins.then_inc(gate_min, 1)
            if (name, i) == ("gv", 1):
                dve.wait_ge(gate_ln, 1)
                own.done(dve.tensor_tensor(lat[:], mn[:], lat[:], ALU.subtract))
            if (name, i) == ("gv", 2):
                dve.wait_ge(zero_done, 3)
                fl = [t[:].rearrange("p k t -> p (k t)") for t in (mn, segm, lat)]
                own.done(dve.tensor_tensor_scan(fl[0], fl[1], fl[2], 0.0, ALU.mult, ALU.add))
            if (name, i) == ("gv", 3):
                by = [t[:].rearrange("p k (c s) -> p (k c) s", s=CHUNK) for t in (lat, mn)]
                n = LKT * NCH
                dve.tensor_tensor(by[0], by[1][:, :, CHUNK - 1:CHUNK].to_broadcast([P, n, CHUNK]), by[1],
                                  ALU.subtract).then_inc(suffix_done, 1)
                own.done(dve.tensor_copy(btot[:, 0], mn[:, :, CHUNK - 1]))
                for c in range(1, NCH):
                    own.done(dve.tensor_tensor(btot[:, c], btot[:, c - 1], mn[:, :, (c + 1) * CHUNK - 1], ALU.add))
                for k, (cs, ct) in enumerate(CHUNK_PAIRS):
                    ins = dve.tensor_tensor(dec[:, k], btot[:, ct], btot[:, cs], ALU.subtract)
                ins.then_inc(dec_diff, 1)
            if (name, i) == ("gv", 4):
                dve.wait_ge(suffix_exp, 1)
                own.done(dve.tensor_tensor(kT[:], kT[:], lat[:], ALU.mult))
            step = {"gq": i, "gr": 4 + i}.get(name, 99)
            if step <= 3:
                if step == 0:
                    dve.wait_ge(dec_done, 1)
                if step >= 2:
                    dve.wait_ge(sc_mm, step - 1)
                for dt in range(2):
                    for k, (cs, ct) in enumerate(CHUNK_PAIRS):
                        ins = dve.tensor_scalar(keys_dec[:, step % 2, dt, k], kT[:, 2 * step + dt, cs * CHUNK:(cs + 1) * CHUNK],
                                                dec[:, k, 2 * step + dt:2 * step + dt + 1], None, ALU.mult)
                ins.then_inc(kd_ready, 1)
            if 3 <= step <= 6:
                hd = step - 3
                dve.wait_ge(ostd_done, hd + 1)
                own.done(dve.reciprocal(rres[:], rtmp[:]))
                own.done(dve.tensor_tensor(osb[:, 4 * hd:4 * hd + 4], osb[:, 4 * hd:4 * hd + 4], bc(rres, 4), ALU.mult))
            if 2 <= step <= 5:
                dve.wait_ge(o_copied, step - 1)
                dve.tensor_tensor(osq[:, 0:2], osq[:, 0:2], osq[:, 2:4], ALU.add).then_inc(osum_done, 1)

        def inv_rms(std_no):
            dve.wait_ge(std_done, std_no)
            dve.reciprocal(rstd[:], rtmp[:]).then_inc(rstd_done, 1)
            dve.wait_ge(rstd_done, std_no)

        def gla(name, i, b, rnd, g):
            take(b, rnd, 0, 4, g)
            if (name, i) == ("gk", 0):
                inv_rms(1)
            if name == "gk":
                own.done(scaled(kT[:, 2 * i:2 * i + 2]))
            if name == "gq":
                own.done(scaled(qT[:, 2 * i:2 * i + 2], DK ** -0.5))
            if name == "gv":
                for j in range(TT):
                    ins = dve.tensor_scalar(vtok[:, j, i * NB:(i + 1) * NB], z[:, j], rcol[:, j:j + 1], None, ALU.mult)
                own.done(ins)
            if name == "gr":
                scaled(z[:]).then_inc(f_in, 1)
                dve.wait_ge(f_in, FUN0["gr"] + i + 1)
                for j in range(2):
                    kt = 2 * i + j
                    ins = dve.scalar_tensor_tensor(out=h[:, j], in0=osb[:, kt], scalar=prm("gla_o_norm", kt % 4), in1=z[:, j],
                                                   op0=ALU.mult, op1=ALU.mult)
                own.done(ins)
                dve.wait_ge(f_out, FUN0["gr"] + i + 1)
                dve.tensor_tensor(h[:], h[:], fo[:], ALU.mult).then_inc(value_ready, 1)
            last_split(rnd, 0, 4)
            if name == "gr":
                emit(PAIR0["gr"] + i, hs, i)
            gla_hooks(name, i)

        straight_walk(GLA_A, gla)

        def add_residual(i):
            own.done(dve.tensor_tensor(pair(xres, i), pair(xres, i), z[:], ALU.add))

        def out_proj(name, pairs0, gain):
            with own.loop(0, 4, 2) as p:
                for g in range(2):
                    i = 2 * p + g
                    take(BLOCK0[name] + i, ROUND0[name] + i, 0, 4, g)
                    add_residual(i)
                    gained(i, gain)
                    last_split(ROUND0[name] + i, 0, 4)
                    emit(pairs0 + i, xs, i)

        out_proj("go", PAIR0["xm1"], "mlp_norm")

        def mlp(name, h_base, std_no, gain, pairs0):
            def up(c, i, b, rnd, g, first=False):
                take(b, rnd, 0, 4, g)
                if first and g == 0:
                    inv_rms(std_no)
                own.done(scaled(h[:]))
                dve.scalar_tensor_tensor(out=z[:], in0=h[:], scalar=0.0, in1=h[:], op0=ALU.max,
                                         op1=ALU.mult).then_inc(value_ready, 1)
                last_split(rnd, 0, 4)
                emit(h_base + 8 * c + i, hs, i, src=z)

            def down(c, i, b, rnd, g, last=False):
                take(b, rnd, 0, 4, g)
                add_residual(i)
                if last:
                    if pairs0 == FINAL0 and not (isinstance(i, int) and i == 0):
                        dve.wait_ge(y_mm, i)
                    gained(i, gain)
                last_split(rnd, 0, 4)
                if last and pairs0 != FINAL0:
                    emit(pairs0 + i, xs, i)

            mlp_walk(loop, name, up, down)

        mlp("m1", PAIR0["h1"], 2, "gmix", PAIR0["x2"])

        def l2_hooks(name, i):
            if name == "q":
                for kt in range(4 * i, 4 * i + 4):
                    ins = dve.scalar_tensor_tensor(out=xres[:, kt], in0=xres[:, kt], scalar=prm("final_norm", kt), in1=rres[:],
                                                   op0=ALU.mult, op1=ALU.mult)
                own.done(ins)
            order = {"xr": 0, "scc": 4, "scx": 8, "br": 12}
            if name not in order:
                return
            s = order[name] + i
            if s < AH:
                dve.wait_ge(qk_mm, s + 1)
                if s == 0:
                    dve.wait_ge(skew_landed, 16 * AH)
                else:
                    dve.wait_ge(at_mm, s)
                dve.scalar_tensor_tensor(out=attn[:, 0:P], in0=flat[1][:, 0:P], scalar=AD ** -0.5, in1=skew[:, s, P:T],
                                         op0=ALU.mult, op1=ALU.add)
                own.done(dve.scalar_tensor_tensor(out=attn[:, P:BW], in0=flat[1][:, P:BW], scalar=AD ** -0.5,
                                                  in1=skew[:, s], op0=ALU.mult, op1=ALU.add))
                dve.tensor_reduce(amax[:, 0:1], attn[:, 0:P], AX_X, ALU.max)
                own.done(dve.tensor_reduce(amax[:, 1:2], attn[:, P:BW], AX_X, ALU.max))
                dve.tensor_scalar(amax[:], amax[:], -1.0, None, ALU.mult).then_inc(attn_max, 1)
            if 2 <= s <= AH + 1:
                dve.wait_ge(ya_hi, s - 1)
                dve.tensor_tensor(hs[:, s - 2, 1], M[3][:, 0], hs[:, s - 2, 0].bitcast(F32),
                                  ALU.subtract).then_inc(ya_done, 1)
            if 4 <= s < 12 and (s - 4) % 2:
                li = (s - 4) // 2
                dve.wait_ge(lru_v, 2 * li + 1)
                dve.scalar_tensor_tensor(out=lru_t[:], in0=gate_a[:], scalar=1.0, in1=lru_t[:], op0=ALU.add,
                                         op1=ALU.mult).then_inc(lru_s, 1)
                own.done(dve.tensor_tensor(gate_x[:], gate_x[:], pair(xc, li), ALU.mult))
            if s < AH:
                dve.wait_ge(attn_exp, s + 1)
                own.done(dve.reciprocal(ainv[:], asum[:]))
                dve.tensor_scalar(attn[:, 0:P], attn[:, 0:P], ainv[:, 0:1], None, ALU.mult)
                dve.tensor_scalar(attn[:, P:BW], attn[:, P:BW], ainv[:, 1:2], None, ALU.mult).then_inc(attn_ready, 1)
            if 6 <= s <= 12 and s % 2 == 0:
                li = (s - 6) // 2
                dve.wait_ge(lru_v, 2 * li + 2)
                own.done(dve.tensor_tensor(gate_x[:], gate_x[:], lru_u[:], ALU.mult))
                for j in range(2):
                    ins = dve.tensor_tensor_scan(xc[:, 2 * li + j], lru_a[:, j], gate_x[:, j], 0.0, ALU.mult, ALU.add)
                ins.then_inc(lru_done, 1)
                dve.wait_ge(lru_done, li + 1)

        def conv(dst, j, width, weight, shift, bias=None):
            for k in range(width):
                src = xpad[:, j, shift + k:shift + k + T]
                if k == 0:
                    w = prm(weight[0], weight[1])
                    if bias is not None:
                        ins = dve.tensor_scalar(dst, src, w, bias, ALU.mult, ALU.add)
                    else:
                        ins = dve.tensor_scalar(dst, src, w, None, ALU.mult)
                else:
                    ins = dve.scalar_tensor_tensor(out=dst, in0=src, scalar=prm(weight[0], weight[1] + k * LKT), in1=dst,
                                                   op0=ALU.mult, op1=ALU.add)
                if k < width - 1:
                    own.done(ins)
            return ins

        def second(name, i, b, rnd, g):
            take(b, rnd, 0, 4, g)
            if (name, i) == ("q", 0):
                dve.wait_ge(std_done, 3)
                own.done(dve.reciprocal(rres[:], rtmp[:]))
                own.done(dve.tensor_tensor(rstd[:], rres[:], rres[:], ALU.mult))
                dve.tensor_tensor(rstd[:], rstd[:], M[0][:, 1], ALU.mult).then_inc(rstd_done, 1)
                dve.wait_ge(std_done, 4)
                own.done(dve.reciprocal(rstd[:], rtmp[:]))
                dve.tensor_tensor(rstd[:], rstd[:], rres[:], ALU.mult).then_inc(rstd_done, 1)
                dve.wait_ge(rstd_done, 4)
            if name in ("q", "k"):
                scaled(pair(q2 if name == "q" else k2, i)).then_inc(qkv_ready, 1)
                dve.wait_ge(qkv_ready, i + 1 + (4 if name == "k" else 0))
            if name == "v":
                if i == 0:
                    dve.wait_ge(rcol_mm, 2)
                    own.done(dve.tensor_copy(rcol[:], M[2][:, :, 0]))
                for j in range(TT):
                    ins = dve.tensor_scalar(v2[:, j, i * NB:(i + 1) * NB], z[:, j], rcol[:, j:j + 1], None, ALU.mult)
                ins.then_inc(qkv_ready, 1)
                dve.wait_ge(qkv_ready, 9 + i)
            if name == "xr":
                if i == 0:
                    dve.wait_ge(zero_done, 2)
                own.done(scaled(xpad[:, :, CONV - 1:]))
                for j in range(2):
                    kt = 2 * i + j
                    ins = conv(xc[:, kt], j, CONV, ("lru_conv_w_2", kt), 0, prm("lru_conv_b_2", kt))
                ins.then_inc(xc_ready, 1)
                dve.wait_ge(xc_ready, i + 1)
            if name == "scc":
                own.done(scaled(pair(cc, i)))
            if name == "scx":
                own.done(scaled(h[:]))
                own.done(dve.tensor_tensor(xpad[:, :, CONV - 1:], h[:], pair(cc, i), ALU.mult))
                for j in range(2):
                    kt = 2 * i + j
                    ins = conv(cc[:, kt], j, SCONV, ("sc_conv_w_2", kt), 1)
                own.done(ins)
            if name == "br":
                scaled(z[:]).then_inc(f_in, 1)
                dve.wait_ge(f_out, FUN0["br"] + i + 1)
                dve.tensor_tensor(h[:], fo[:], pair(xc, i), ALU.mult).then_inc(value_ready, 1)
            if name == "scb":
                own.done(scaled(z[:]))
                dve.tensor_tensor(h[:], z[:], pair(cc, i), ALU.mult).then_inc(value_ready, 1)
            last_split(rnd, 0, 4)
            if name == "br":
                emit(PAIR0["yb"] + i, hs, 4 + i)
            if name == "scb":
                emit(PAIR0["yc"] + i, ycs, i)
            l2_hooks(name, i)

        straight_walk(L2_A, second)

        def mix(j, n, b, rnd, first, units, g):
            branch = j // 2
            if j % 2:
                dve.wait_ge(f_out, FUN0["gate"] + 3 * n + branch + 1)
            take(b, rnd, first, units, g)
            if j % 2 == 0:
                scaled(z[:]).then_inc(f_in, 1)
            elif branch == 0:
                own.done(dve.tensor_tensor(h[:], z[:], fo[:], ALU.mult))
            else:
                own.done(dve.tensor_tensor(z[:], z[:], fo[:], ALU.mult))
                ins = dve.tensor_tensor(h[:], h[:], z[:], ALU.add)
                if branch == 2:
                    ins.then_inc(value_ready, 1)
                else:
                    own.done(ins)
            last_split(rnd, first, units)
            if j == 5:
                emit(PAIR0["mix"] + n, mixs, n)

        mix_walk(loop, mix)
        out_proj("lo", PAIR0["xm2"], "norm_mlp_g_2")
        mlp("m2", PAIR0["h2"], 5, "final_g_2", FINAL0)
        dve.wait_ge(std_done, 6)
        own.done(dve.reciprocal(rcol[:], rcol[:]))
        dve.wait_ge(y_copied, PAIRS)
        for j in range(TT):
            for half in range(2):
                part = ytok[:, j, half * 1024:half * 1024 + 1024]
                dve.tensor_scalar(part, part, rcol[:, j:j + 1], None, ALU.mult).then_inc(y_scaled, 1)

    return ctx


NAMES = ["x", "gla_norm", "gla_w_in", "gla_w_gate_up", "gla_b_gate", "gla_o_norm", "gla_w_out", "mlp_norm",
         "mlp_w_up", "mlp_w_down", "final_norm", "norm_mix_g_2", "w_in_2", "gate_b_2", "rel_table_2", "w_attn_o_2",
         "lru_conv_w_2", "lru_conv_b_2", "lru_wa_2", "lru_ba_2", "lru_wx_2", "lru_bx_2", "lru_lambda_2", "w_lru_o_2",
         "sc_conv_w_2", "w_sc_o_2", "w_out_2", "norm_mlp_g_2", "w_mlp_up_2", "w_mlp_down_2", "final_g_2"]


def kernel(**inputs):
    import concourse.bacc as bacc
    from concourse.bass_utils import run_bass_kernel_spmd

    nc = bacc.Bacc("TRN2", target_bir_lowering=False, num_devices=1,
                   dynamic_dma_scratch_size=4096)
    arrays, aps = {}, {}
    for name in NAMES:
        v = np.ascontiguousarray(inputs[name])
        if name in ROWS:
            v = v.reshape(-1)
        elif name in ("lru_wa_2", "lru_wx_2"):
            v = v.reshape(v.shape[1:])
        elif name != "rel_table_2":
            v = v.reshape(v.shape[-2:])
        arrays[f"in_{name}"] = v
    arrays["in_onehot"] = bucket_rows()
    for name, v in arrays.items():
        aps[name[3:]] = nc.dram_tensor(name, v.shape, mybir.dt.from_np(v.dtype), kind="ExternalInput").ap()
    out = nc.dram_tensor("out_dram", (T, D), F32, kind="ExternalOutput").ap()
    scratch = nc.dram_tensor("bias_scratch", (AH * P * BW,), F32, kind="Internal").ap()
    with build(nc, aps, out, scratch):
        pass
    r = run_bass_kernel_spmd(nc, [arrays], core_ids=[0])
    return r.results[0]["out_dram"].reshape(1, T, D)
```
